# Optimizing a Trainium2 kernel written in Bass

```python
import math
import jax, jax.numpy as jnp
from jax import lax
import numpy as np

D_MODEL = 1024
BATCH = 1
SEQ = 1024
DEPTH = 2

GRID_W = 64
CTX_LEN = 256
N_MIXERS = 2
MIXER_MLA = 0
MIXER_CONV = 1
N_HEADS = 8
QK_NOPE = 128
QK_ROPE = 64
V_HEAD = 128
Q_LORA = 256
KV_LORA = 128
CONV_W = 3
D_FF = ((8 * D_MODEL + 3 * 256 - 1) // (3 * 256)) * 256
ROPE_THETA = 10000.0
NORM_EPS = 1e-6
Q_BLOCK = 128
ATTN_SCALE = 1.0 / math.sqrt(QK_NOPE + QK_ROPE)
N_MLA_LAYERS = (DEPTH + N_MIXERS - 1) // N_MIXERS
N_CONV_LAYERS = DEPTH // N_MIXERS

kernel_name = "hybrid_mla_shortconv_dit_block"

def rmsnorm(x, w):
    xf = x.astype(jnp.float32)
    y = xf * lax.rsqrt(jnp.mean(xf * xf, axis=-1, keepdims=True) + NORM_EPS)
    return (y * w.astype(jnp.float32)).astype(x.dtype)

def modulate(h, shift, scale):
    return h * (1 + scale) + shift

def axial_angles(n_tok):
    rows = n_tok // GRID_W
    row, col = jnp.meshgrid(jnp.arange(rows), jnp.arange(GRID_W), indexing="ij")
    row = row.reshape(-1).astype(jnp.float32)
    col = col.reshape(-1).astype(jnp.float32)
    n_freq = QK_ROPE // 4
    freqs = ROPE_THETA ** (-jnp.arange(n_freq, dtype=jnp.float32) / n_freq)
    return row[:, None] * freqs, col[:, None] * freqs

def rotate_half(x, ang):
    x1, x2 = jnp.split(x, 2, axis=-1)
    cos, sin = jnp.cos(ang), jnp.sin(ang)
    return jnp.concatenate([x1 * cos - x2 * sin, x2 * cos + x1 * sin], axis=-1)

def axial_rope(x, ang_row, ang_col):
    extra = x.ndim - 3
    shp = (ang_row.shape[0],) + (1,) * extra + (ang_row.shape[1],)
    xr, xc = jnp.split(x.astype(jnp.float32), 2, axis=-1)
    out = jnp.concatenate([rotate_half(xr, ang_row.reshape(shp)),
                           rotate_half(xc, ang_col.reshape(shp))], axis=-1)
    return out.astype(x.dtype)

def mla_qkv(h, w_dq, q_norm, w_uq, w_dkv, kv_norm, w_ukv):
    b, n, _ = h.shape
    q = (rmsnorm(h @ w_dq, q_norm) @ w_uq).reshape(b, n, N_HEADS, QK_NOPE + QK_ROPE)
    kv_a = h @ w_dkv
    kv = (rmsnorm(kv_a[..., :KV_LORA], kv_norm) @ w_ukv).reshape(b, n, N_HEADS, QK_NOPE + V_HEAD)
    return (q[..., :QK_NOPE], q[..., QK_NOPE:],
            kv[..., :QK_NOPE], kv_a[..., KV_LORA:], kv[..., QK_NOPE:])

def attend(q_nope, q_rope, k_nope, k_rope, v):
    s = (jnp.einsum("bqhd,bkhd->bhqk", q_nope, k_nope)
         + jnp.einsum("bqhr,bkr->bhqk", q_rope, k_rope))
    p = jax.nn.softmax(s.astype(jnp.float32) * ATTN_SCALE, axis=-1).astype(v.dtype)
    return jnp.einsum("bhqk,bkhd->bqhd", p, v)

def mla_mixer(h_lat, h_ctx, w_dq, q_norm, w_uq, w_dkv, kv_norm, w_ukv, w_o,
              ang_row, ang_col, with_ctx_out):
    b, n, _ = h_lat.shape
    qn_l, qr_l, kn_l, kr_l, v_l = mla_qkv(h_lat, w_dq, q_norm, w_uq, w_dkv, kv_norm, w_ukv)
    qr_l = axial_rope(qr_l, ang_row, ang_col)
    kr_l = axial_rope(kr_l, ang_row, ang_col)
    qn_c, qr_c, kn_c, kr_c, v_c = mla_qkv(h_ctx, w_dq, q_norm, w_uq, w_dkv, kv_norm, w_ukv)
    k_nope = jnp.concatenate([kn_c, kn_l], axis=1)
    k_rope = jnp.concatenate([kr_c, kr_l], axis=1)
    v = jnp.concatenate([v_c, v_l], axis=1)
    nb = n // Q_BLOCK

    def to_blocks(t):
        return jnp.moveaxis(t.reshape(b, nb, Q_BLOCK, *t.shape[2:]), 1, 0)

    o = lax.map(lambda q: attend(q[0], q[1], k_nope, k_rope, v), (to_blocks(qn_l), to_blocks(qr_l)))
    o = jnp.moveaxis(o, 0, 1).reshape(b, n, N_HEADS * V_HEAD)
    y_lat = o @ w_o
    y_ctx = None
    if with_ctx_out:
        o_c = attend(qn_c, qr_c, kn_c, kr_c, v_c)
        y_ctx = o_c.reshape(b, h_ctx.shape[1], N_HEADS * V_HEAD) @ w_o
    return y_lat, y_ctx

def short_conv(h, w_in, w_conv, w_out):
    b_g, c_g, xv = jnp.split(h @ w_in, 3, axis=-1)
    u = lax.conv_general_dilated(c_g * xv, w_conv[:, None, :], window_strides=(1,),
                                 padding=[(CONV_W // 2, CONV_W // 2)],
                                 dimension_numbers=("NWC", "WIO", "NWC"),
                                 feature_group_count=D_MODEL)
    return (b_g * u) @ w_out

def swiglu(h, w_gate, w_up, w_down):
    return (jax.nn.silu(h @ w_gate) * (h @ w_up)) @ w_down

def setup_inputs(seed: int = 0) -> dict:
    key = jax.random.key(seed)
    ks = jax.random.split(key, 24)
    f32 = jnp.float32

    def nrm(k, shape, scale):
        return jax.random.normal(k, shape, f32) * scale

    def gain(k, shape):
        return 1.0 + 0.02 * jax.random.normal(k, shape, f32)

    d = D_MODEL
    return {
        "x": nrm(ks[0], (BATCH, SEQ, d), 1.0),
        "c": nrm(ks[1], (BATCH, d), 1.0),
        "ctx": nrm(ks[2], (BATCH, CTX_LEN, d), 1.0),
        "c_ctx": nrm(ks[3], (d,), 1.0),
        "ada_w": nrm(ks[4], (DEPTH, d, 6 * d), 0.5 * d ** -0.5),
        "ada_b": nrm(ks[5], (DEPTH, 6 * d), 0.02),
        "norm_mix": gain(ks[6], (DEPTH, d)),
        "norm_ffn": gain(ks[7], (DEPTH, d)),
        "mla_w_dq": nrm(ks[8], (N_MLA_LAYERS, d, Q_LORA), d ** -0.5),
        "mla_q_norm": gain(ks[9], (N_MLA_LAYERS, Q_LORA)),
        "mla_w_uq": nrm(ks[10], (N_MLA_LAYERS, Q_LORA, N_HEADS * (QK_NOPE + QK_ROPE)), Q_LORA ** -0.5),
        "mla_w_dkv": nrm(ks[11], (N_MLA_LAYERS, d, KV_LORA + QK_ROPE), d ** -0.5),
        "mla_kv_norm": gain(ks[12], (N_MLA_LAYERS, KV_LORA)),
        "mla_w_ukv": nrm(ks[13], (N_MLA_LAYERS, KV_LORA, N_HEADS * (QK_NOPE + V_HEAD)), KV_LORA ** -0.5),
        "mla_w_o": nrm(ks[14], (N_MLA_LAYERS, N_HEADS * V_HEAD, d), (N_HEADS * V_HEAD) ** -0.5),
        "conv_w_in": nrm(ks[15], (N_CONV_LAYERS, d, 3 * d), d ** -0.5),
        "conv_w": nrm(ks[16], (N_CONV_LAYERS, CONV_W, d), CONV_W ** -0.5),
        "conv_w_out": nrm(ks[17], (N_CONV_LAYERS, d, d), d ** -0.5),
        "ffn_w_gate": nrm(ks[18], (DEPTH, d, D_FF), d ** -0.5),
        "ffn_w_up": nrm(ks[19], (DEPTH, d, D_FF), d ** -0.5),
        "ffn_w_down": nrm(ks[20], (DEPTH, D_FF, d), D_FF ** -0.5),
        "final_norm": gain(ks[21], (d,)),
    }

def reference(x, c, ctx, c_ctx, ada_w, ada_b, norm_mix, norm_ffn,
              mla_w_dq, mla_q_norm, mla_w_uq, mla_w_dkv, mla_kv_norm, mla_w_ukv, mla_w_o,
              conv_w_in, conv_w, conv_w_out, ffn_w_gate, ffn_w_up, ffn_w_down, final_norm):
    d = D_MODEL
    ang_row, ang_col = axial_angles(x.shape[1])
    silu_c = jax.nn.silu(c)
    silu_cc = jax.nn.silu(c_ctx)
    for i in range(DEPTH):
        mixer = i % N_MIXERS
        j = i // N_MIXERS
        ctx_live = any(k % N_MIXERS == MIXER_MLA for k in range(i + 1, DEPTH))
        sh1, sc1, g1, sh2, sc2, g2 = jnp.split((silu_c @ ada_w[i] + ada_b[i])[:, None, :], 6, axis=-1)
        n_ctx_mod = 6 if ctx_live else (2 if mixer == MIXER_MLA else 0)
        mc = None
        if n_ctx_mod:
            mc = jnp.split(silu_cc @ ada_w[i][:, :n_ctx_mod * d] + ada_b[i][:n_ctx_mod * d], n_ctx_mod)
        h = modulate(rmsnorm(x, norm_mix[i]), sh1, sc1)
        if mixer == MIXER_MLA:
            h_c = modulate(rmsnorm(ctx, norm_mix[i]), mc[0], mc[1])
            y, y_c = mla_mixer(h, h_c, mla_w_dq[j], mla_q_norm[j], mla_w_uq[j], mla_w_dkv[j],
                               mla_kv_norm[j], mla_w_ukv[j], mla_w_o[j], ang_row, ang_col, ctx_live)
        else:
            y = short_conv(h, conv_w_in[j], conv_w[j], conv_w_out[j])
            y_c = None
            if ctx_live:
                h_c = modulate(rmsnorm(ctx, norm_mix[i]), mc[0], mc[1])
                y_c = short_conv(h_c, conv_w_in[j], conv_w[j], conv_w_out[j])
        x = x + g1 * y
        x = x + g2 * swiglu(modulate(rmsnorm(x, norm_ffn[i]), sh2, sc2),
                            ffn_w_gate[i], ffn_w_up[i], ffn_w_down[i])
        if ctx_live:
            ctx = ctx + mc[2] * y_c
            ctx = ctx + mc[5] * swiglu(modulate(rmsnorm(ctx, norm_ffn[i]), mc[3], mc[4]),
                                       ffn_w_gate[i], ffn_w_up[i], ffn_w_down[i])
    return rmsnorm(x, final_norm)


_drawn_inputs = setup_inputs


def setup_inputs(seed=0):
    import zlib

    import numpy as np

    out = dict(_drawn_inputs(seed))
    spreads = {}
    factors = {'ctx': 6.91,
     'norm_mix': 4.946,
     'norm_ffn': 6.331,
     'mla_q_norm': 8.0,
     'mla_kv_norm': 8.0,
     'final_norm': 2.752}
    for name, (base, spread) in spreads.items():
        noise = np.random.default_rng([zlib.crc32(name.encode()), seed]).standard_normal(out[name].shape)
        drawn = base * np.exp(spread * noise) if base else spread * noise
        out[name] = __import__('jax').numpy.asarray(drawn.astype(out[name].dtype))
    for name, factor in factors.items():
        out[name] = (out[name] * factor).astype(out[name].dtype)
    return out
```

```python
from collections import defaultdict
from contextlib import ExitStack

import numpy as np

import concourse.bass as bass
from concourse import mybir

F32 = mybir.dt.float32
F32R = mybir.dt.float32r
ALU = mybir.AluOpType
ACT = mybir.ActivationFunctionType
AX_X = mybir.AxisListType.X

P = 128
D = 1024
T = 1024
TC = 256
TK = T + TC
KD = D // P
HT = 512
HEADS = 8
NOPE, ROPE, VH = 128, 64, 128
QL, KVL = 256, 128
QK = QL // P
FF = 2816
FFN_BLOCKS = FF // (2 * P)
CONV_BLOCKS = D // (2 * P)
OUT_BLOCKS = HEADS // 2
EPS = 1e-6
SCALE = float(1.0 / np.sqrt(NOPE + ROPE))
KT = TK // P
HW = 2 * P + P + 2 * P
SHIFT1, SCALE1, GATE1, SHIFT2, SCALE2, GATE2 = range(6)
N_PE_MOD = 2 * KD
N_ATT_MOD = 4 * KD
PRO_TILES = 4
MASK16 = [(p + 16) % 32 for p in range(32)]


def mod_col(layer, group):
    return (layer * 6 + group) * KD


class Counts:

    def __init__(self):
        self.n, self.i, self.per, self.start = defaultdict(int), None, {}, {}

    def add(self, name, k=1):
        self.n[name] += k

    def at(self, name, back=0):
        v = self.n[name] - back
        per = self.per.get(name, 0) if self.i is not None else 0
        return self.i * per + v if per else v

    def enter(self, i, per):
        self.i, self.per, self.start = i, per, dict(self.n)

    def leave(self, passes):
        for name, v in list(self.n.items()):
            rise = v - self.start.get(name, 0)
            assert rise == self.per.get(name, 0), (name, rise)
            self.n[name] = self.start.get(name, 0) + rise * passes
        self.i = None


RING_KINDS = ("T", "OH", "B", "W", "R", "Q")


def group_script(scores, query_stage):
    stage = {1: ("W", 0), 2: ("R", 0), 3: ("R", 1), 4: ("Q", 0), 5: ("Q", 1)} if query_stage else {}
    items = [("T", 0), ("T", 1), "S", "S", ("OH", 0), ("B", 0)]
    for k in range(KT):
        items.append(("PV", k))
        if k in stage:
            items.append(stage[k])
        if k + 2 < KT:
            items.append(("T", k + 2))
        if k < 5:
            items += ["S", "S"]
    out, n, due = [], 0, []
    for item in items:
        if item != "S":
            out.append((*item, 0))
            if item[0] in RING_KINDS:
                due = [(left - 1, *entry) for left, *entry in due]
                out += [(*entry, 0) for left, *entry in due if left == 0]
                due = [d for d in due if d[0] > 0]
        elif scores:
            out.append(("S", n // 3, n % 3))
            if n % 3 == 2:
                out.append(("M", n // 3, 0))
                due += [(1, "X", n // 3), (2, "V", n // 3)]
            n += 1
    return out + [(*entry, 0) for _, *entry in due]


QUERY_STAGE = (("W", 0), ("R", 0), ("R", 1), ("Q", 0), ("Q", 1))
SPLIT_KINDS = {"T", "W", "Q"}
NORM_AT = {4: 0, 8: 1, 12: 2}
MOD_AT = {5: 0, 7: 1}


def script_of(gb, last):
    return group_script(not (last and gb == 3), has_query(gb, last))


def has_query(gb, last):
    return gb % 2 == 0 and not (last and gb == 2)


def value_parity(gb):
    return 1 if gb in (0, 3) else 0


J_CTX, J_XA, J_XB, J_KVC, J_KVA, J_QA, J_KVB, J_QB, J_MIX = range(9)


def job_cols(j):
    return TC if j in (J_CTX, J_KVC) else HT


def job_n(j):
    return {J_KVC: KVL, J_KVA: KVL, J_KVB: KVL, J_QA: QL, J_QB: QL}.get(j, D)


def job_banks(j):
    if j < J_MIX:
        return 6, 7
    return (2, 3) if j % 2 == 0 else (4, 5)


PHASES = [("out", OUT_BLOCKS, 0, mod_col(0, GATE1)),
          ("ffn", FFN_BLOCKS, OUT_BLOCKS, mod_col(0, GATE2)),
          ("conv", CONV_BLOCKS, OUT_BLOCKS + FFN_BLOCKS, mod_col(1, GATE1)),
          ("ffn", FFN_BLOCKS, OUT_BLOCKS + FFN_BLOCKS + CONV_BLOCKS, mod_col(1, GATE2))]
AFTER = [(mod_col(0, SHIFT2), 2), (mod_col(1, SHIFT1), 3), (mod_col(1, SHIFT2), 4)]
OUT_TILES = [[(4, 0), (5, 0)], [(6, 0), (7, 0)], [(4, 1), (5, 1)], [(0, 0), (1, 0)], [(6, 2), (7, 2)],
             [(2, 0), (3, 0)], [(4, 3), (5, 3)]]
OUT_NEEDS = [2, 4, 6, 10]
N_OUT_TILES = sum(map(len, OUT_TILES))
RING_PASS, SPLIT_PASS = 58, 46
LAST_QUERY = 5 + RING_PASS * (HEADS // 2 - 1) + KT + 2 + 5
RING_ALL = 5 + RING_PASS * (HEADS // 2) - 5 + 1


def build(nc, x_t, ctx_t, cc, c_row, ada_pe, ada_rows, vec, consts, rope, head_w, stream, out_t):
    ctx = ExitStack()
    base = (nc.sbuf_base + 31) // 32 * 32

    def sb(name, shape, dt, at):
        assert base + at + 4 * int(np.prod(shape)) <= nc.sbuf_usable_end, name
        return nc.alloc_sbuf_tensor_at(name, [P, *shape], dt, offset=base + at)

    def pair(name, shape, at):
        return sb(name + "_hi", shape, F32R, at), sb(name + "_lo", shape, F32R, at + 4 * int(np.prod(shape)))

    ident = sb("ident", [P], F32, 0)
    ones = sb("ones", [P], F32, 512)
    mods = sb("mods", [96], F32, 1024)
    vecs = sb("vecs", [163], F32, 1408)
    ctx_mod = sb("ctx_mod", [16], F32, 2080)
    svec = sb("svec", [5, KD], F32, 2144)
    silu_cc = sb("silu_cc", [KD, 2], F32, 2336)
    cc_sb = sb("cc_sb", [KD, 2], F32, 2400)
    eps_c = sb("eps_c", [1], F32, 2464)
    sd = sb("sd", [4], F32, 2496)
    rr = sb("rr", [4], F32, 2528)
    mod_new = sb("mod_new", [8], F32, 2560)
    nmax = sb("nmax", [2], F32, 2592)
    rsum = sb("rsum", [8], F32, 2624)
    rinv = sb("rinv", [8], F32, 2656)
    mx_raw = sb("mx_raw", [2], F32, 2688)
    taps = sb("taps", [3], F32, 2720)
    B0 = 3072
    adab, norm_w = vecs[:, 0:96], vecs[:, 96:136]
    qn_w, kvn_w, conv_w = vecs[:, 136:138], vecs[:, 138:139], vecs[:, 139:163]
    x = sb("x", [KD, T], F32, B0)
    pt_hi, pt_lo = pair("pt", [4, HT], B0)
    mod_raw = sb("mod_raw", [2, D], F32, B0 + 16384)
    mod_prod = sb("mod_prod", [D], F32, B0 + 24576)
    row_a = sb("row_a", [D], F32, B0 + 28672)
    H0 = B0 + 32768
    hb0 = pair("hb0", [KD, HT], H0)
    o = sb("o", [1 + 2 * HEADS, HT], F32, H0)
    K0 = H0 + 34816
    ckv_hi, ckv_lo = pair("ckv", [TK], K0)
    kr_hi, kr_lo = pair("kr", [TK], K0 + 10240)
    qn_hi, qn_lo = pair("qn", [QK, T], K0 + 20480)
    tab = sb("tab", [2, T], F32, K0 + 36864)
    A0 = K0 + 45056
    hb1 = pair("hb1", [KD, HT], A0)
    ada_ring = sb("ada_ring", [8, D], F32, A0)
    pw = pair("pw", [PRO_TILES, D], A0 + 32768)
    R0 = A0 + 65536
    rsb = [sb(f"rsb{k}", [HT], F32, R0 + 2048 * k) for k in range(2)]
    rsh = [sb(f"rsh{k}", [HT], F32, R0 + 4096 + 2048 * k) for k in range(2)]
    diag = sb("diag", [4, P], F32, R0 + 8192)
    N0 = R0 + 10240
    sq = [sb(f"sq{k}", [HT], F32, N0 + 2048 * k) for k in range(2)]
    acc = [sb(f"acc{k}", [HT], F32, N0 + 4096 + 2048 * k) for k in range(2)]
    rstd = [sb(f"rstd{k}", [HT], F32, N0 + 8192 + 2048 * k) for k in range(2)]
    tmp = [sb(f"tmp{k}", [HT], F32, N0 + 12288 + 2048 * k) for k in range(2)]
    W1 = N0 + 16384
    raw = [sb(f"raw{k}", [D], F32, W1 + 4096 * k) for k in range(2)]
    X0 = W1 + 8192
    ctx_sb = sb("ctx_sb", [KD, TC], F32, X0)
    kvf = sb("kvf", [TK], F32, X0)
    pbuf = sb("pbuf", [8, TK], F32, A0)
    tok_hi, tok_lo = pair("tok", [KT, P], A0 + 40960)
    olat_hi, olat_lo = pair("olat", [HT], A0 + 51200)
    qa = [pair(f"qa{p}", [T], A0 + 55296 + 12288 * p) for p in range(2)]
    qr = [sb(f"qr{p}", [T], F32R, A0 + 55296 + 12288 * p + 8192) for p in range(2)]
    Q0 = A0 + 79872
    qsb = [sb(f"qsb{k}", [HT], F32, Q0 + 2048 * k) for k in range(2)]
    qsh = [sb(f"qsh{k}", [HT], F32, Q0 + 4096 + 2048 * k) for k in range(2)]
    inv_diag = sb("inv_diag", [4, P], F32, Q0 + 8192)
    inv_rows = sb("inv_rows", [HT], F32, Q0 + 10240)
    assert Q0 + 12288 <= W1
    olat = sb("olat", [HT], F32, X0 + 9216)
    hraw = sb("hraw", [HW + P], F32, W1)
    hw_hi, hw_lo = pair("hw", [HW], W1 + 3072)
    wa_hi, wa_lo = pair("wa", [QK, P], X0 + 5120)
    uv = [pair(f"uv{p}", [P], X0 + 7168 + 1024 * p) for p in range(2)]
    h = pair("h", [KD, T], H0)
    w_hi, w_lo = pair("w", [8, D], H0 + 65536)
    g_hi, g_lo = pair("g", [2, T], H0 + 131072)
    G1 = H0 + 131072 + 16384
    ab = [sb(f"ab{k}", [HT], F32, G1 + 2048 * k) for k in range(2)]
    assert G1 + 4096 <= R0 + 8192, (G1, R0)
    row_f = sb("row_f", [D], F32, X0)
    mod_raw_f = sb("mod_raw_f", [D], F32, X0 + 4096)
    bsb = sb("bsb", [T], F32, X0)
    zb = sb("zb", [T + 2], F32, X0 + 4096)
    ub = sb("ub", [T], F32, N0)

    ps = ctx.enter_context(nc.psum_tensor("ps", [P, 8, 512], F32))
    flat = ps[:].rearrange("p b n -> p (b n)")

    def sem(name):
        return ctx.enter_context(nc.semaphore("s_" + name))

    in_small, in_ctx, in_tab, in_row = (sem(n) for n in ("in_small", "in_ctx", "in_tab", "in_row"))
    in_x = [sem(f"in_x{k}") for k in range(KD)]
    in_xh = [sem("in_xa"), sem("in_xb")]
    in_ada = [sem(f"in_ada{k}") for k in range(8)]
    in_raw = [sem("in_raw0"), sem("in_raw1")]
    in_mod = [sem("in_mod0"), sem("in_mod1")]
    in_head, in_modf, out_done = sem("in_head"), sem("in_modf"), sem("out_done")
    const_set, silu_done, ada_mm, mod_set, mod_p, mod_c, mod_out, mod_used, sv_set = (
        sem(n) for n in "const_set silu_done ada_mm mod_set mod_p mod_c mod_out mod_used sv_set".split())
    sqd, sqa, st_sum, st_sd, st_dg, st_bc, st_rs, n_mul, n_aff, n_lo = (
        sem(n) for n in "sqd sqa st_sum st_sd st_dg st_bc st_rs n_mul n_aff n_lo".split())
    t_hi, t_lo, pj, dn, xe = (sem(n) for n in ("t_hi", "t_lo", "pj", "dn", "xe"))
    kv_sq, q_sq, q_acc, kr_in, kr_sh, kr_rot, kv_done, kr_done, q_done, tok_t, tok_h, tok_done = (
        sem(n) for n in "kv_sq q_sq q_acc kr_in kr_sh kr_rot kv_done kr_done q_done tok_t tok_h tok_done".split())
    hw_h, hw_l, rg, ra, rd, s_mm, mx, ex, ri, pv, ol_l, q_sh, q_rot, q_ready = (
        sem(n) for n in "hw_h hw_l rg ra rd s_mm mx ex ri pv ol_l q_sh q_rot q_ready".split())
    o_h, sil, gm, cs, zm, gl, fin = (sem(n) for n in ("o_h", "sil", "gm", "cs", "zm", "gl", "fin"))
    v = sem("v")
    wait_end = sem("wait_end")
    gp = sem("gp")

    HALF = (slice(0, HT), slice(HT, T))
    ALL = slice(None)

    def mm3(out, w, wi, a, ai, start, stop):
        nc.tensor.matmul(out, w[0][wi], a[0][ai], start=start, stop=False)
        nc.tensor.matmul(out, w[0][wi], a[1][ai], start=False, stop=False)
        return nc.tensor.matmul(out, w[1][wi], a[0][ai], start=False, stop=stop)

    def tile_of(dram, n):
        return dram[n] if isinstance(n, int) else dram[bass.ds(n, 1)].rearrange("a p n -> p (a n)")

    def cols_of(t, n, width):
        return t[:, n:n + width] if isinstance(n, int) else t[:, bass.ds(n, width)]

    block = ctx.enter_context(nc.Block())

    @block.sync
    def _(sp):
        C = Counts()

        def tile_in(n, k):
            sp.wait_ge(t_lo, C.at("t_lo", 1))
            sp.dma_start(raw[k][:], tile_of(stream, n)).then_inc(in_raw[k], 16)
            C.add("t_lo")

        sp.dma_start(ident[:], consts[:, 0:P]).then_inc(in_small, 16)
        sp.dma_start(ones[:], consts[:, P:2 * P]).then_inc(in_small, 16)
        sp.dma_start(cc_sb[:].rearrange("p k j -> p (k j)"), cc).then_inc(in_small, 16)
        sp.dma_start(vecs[:], vec).then_inc(in_small, 16)
        x_view = x_t.rearrange("(k p) t -> p k t", p=P)
        for m in range(N_PE_MOD):
            if m >= 8:
                sp.wait_ge(ada_mm, m - 7)
            sp.dma_start(ada_ring[:, m % 8, :], ada_pe[m]).then_inc(in_ada[m % 8], 16)
            if m == 1:
                sp.dma_start(ctx_sb[:], ctx_t.rearrange("(k p) t -> p k t", p=P)).then_inc(in_ctx, 16)
            elif m in (3, 5):
                half = (m - 3) // 2
                sp.dma_start(x[:, :, HALF[half]], x_view[:, :, HALF[half]]).then_inc(in_xh[half], 16)
            if m == 7:
                for n in range(2):
                    sp.dma_start(raw[n][:], stream[n]).then_inc(in_raw[n], 16)
        C.add("t_lo", 2)
        sp.dma_start(tab[:].rearrange("p a t -> p (a t)"), rope).then_inc(in_tab, 16)
        for n in range(2, PRO_TILES):
            tile_in(n, n % 2)

        def head_in(n):
            sp.wait_ge(hw_l, C.at("hw_l"))
            sp.dma_start(hraw[:], tile_of(head_w, n)).then_inc(in_head, 16)
            C.add("hw_l")

        def mod_in(n, k):
            sp.wait_ge(mod_p, C.at("mod_p", 1))
            sp.dma_start(mod_raw[:, k, :], tile_of(ada_rows, n)).then_inc(in_mod[k], 16)
            C.add("mod_p")

        sp.wait_ge(t_lo, PRO_TILES)
        sp.dma_start(hraw[:], head_w[0]).then_inc(in_head, 16)
        C.add("hw_l")
        sp.wait_ge(n_lo, 3 * KD)
        sp.dma_start(row_a[:], c_row.partition_broadcast(P)).then_inc(in_row, 16)
        for k in range(2):
            sp.dma_start(mod_raw[:, k, :], ada_rows[k]).then_inc(in_mod[k], 16)
        C.add("mod_p", 2)

        def pass_in(i, last):
            for j in range(2):
                if not (last and j == 1):
                    head_in(i * 2 + (1 + j))
                for k in range(4):
                    if not (last and j == 1 and k >= 2):
                        mod_in(i * 8 + (2 + 4 * j + k), k % 2)

        passes = HEADS // 2 - 1
        with sp.Fori(0, passes) as i:
            C.enter(i, {"hw_l": 2, "mod_p": 8})
            pass_in(i, False)
            C.leave(passes)
        pass_in(passes, True)

        def x_in(k):
            sp.dma_start(x[:, k, :], x_view[:, k, :]).then_inc(in_x[k], 16)

        n0 = PRO_TILES
        for n in range(N_OUT_TILES):
            if n == 0:
                sp.wait_ge(hw_l, HEADS)
                sp.wait_ge(rg, LAST_QUERY)
            tile_in(n0 + n, n % 2)
            if n == 1:
                sp.wait_ge(mod_c, N_ATT_MOD)
                sp.wait_ge(rd, SPLIT_PASS * (passes + 1))
                sp.wait_ge(pv, 4 + 20 * HEADS)
                for k in range(KD):
                    x_in(k)
                sp.wait_ge(rg, RING_ALL)
                sp.wait_ge(ra, RING_ALL)
            if n == 3:
                sp.dma_start(row_f[:], c_row.partition_broadcast(P)).then_inc(in_row, 16)
        n0 += N_OUT_TILES

        def modf_in(n):
            sp.wait_ge(mod_used, C.at("mod_used"))
            sp.dma_start(mod_raw_f[:], tile_of(ada_rows, n)).then_inc(in_modf, 16)
            C.add("mod_used")

        def block_in(n, tiles, mod_n, mod_tiles):
            mods_before = {0: (0, 1), 2: (1, mod_tiles // 2 + 1), 4: (mod_tiles // 2 + 1, mod_tiles)}
            for k in range(tiles):
                if mod_tiles and k in mods_before:
                    for m in range(*mods_before[k]):
                        modf_in(mod_n + m)
                tile_in(n + k, k % 2)

        with sp.Fori(0, FFN_BLOCKS - 1) as i:
            C.enter(i, {"t_lo": 6, "mod_used": 4})
            block_in(i * 6 + n0, 6, i * 4 + N_ATT_MOD, 4)
            C.leave(FFN_BLOCKS - 1)
        n0 += 6 * (FFN_BLOCKS - 1)
        block_in(n0, 6, N_ATT_MOD + 4 * (FFN_BLOCKS - 1), 8)
        n0 += 6
        with sp.Fori(0, CONV_BLOCKS) as i:
            C.enter(i, {"t_lo": 8})
            block_in(i * 8 + n0, 8, 0, 0)
            C.leave(CONV_BLOCKS)
        n0 += 8 * CONV_BLOCKS
        with sp.Fori(0, FFN_BLOCKS - 1) as i:
            C.enter(i, {"t_lo": 6})
            block_in(i * 6 + n0, 6, 0, 0)
            C.leave(FFN_BLOCKS - 1)
        for k in range(2 * KD):
            sp.wait_ge(fin, k + 1)
            cols = HALF[k // KD]
            sp.dma_start(out_t[(k % KD) * P:(k % KD + 1) * P, cols], x[:, k % KD, cols]).then_inc(out_done, 16)
        sp.wait_ge(out_done, 32 * KD)

    @block.tensor
    def _(pe):
        C = Counts()

        def job_sum(j):
            bank = job_banks(j)[0]
            if job_n(j) == D:
                C.add("sqa", KD - 1)
                pe.wait_ge(sqa, C.at("sqa"))
            elif job_n(j) == QL:
                C.add("q_acc")
                pe.wait_ge(q_acc, C.at("q_acc"))
            else:
                C.add("kv_sq")
                pe.wait_ge(kv_sq, C.at("kv_sq"))
            if j >= 1:
                pe.wait_ge(st_sd, j)
            for t in range(job_cols(j) // P):
                last = nc.tensor.matmul(ps[:, bank, t:t + 1], acc[j % 2][:, t * P:(t + 1) * P], ones[:, 0:1],
                                        start=True, stop=True)
            last.then_inc(st_sum, 1)

        def job_bcast(j):
            pe.wait_ge(st_dg, j + 1)
            if j >= 1:
                pe.wait_ge(st_rs, j)
            for t in range(job_cols(j) // P):
                last = nc.tensor.matmul(ps[:, job_banks(j)[1], t * P:(t + 1) * P], ones[:], diag[:, t, :],
                                        start=True, stop=True)
            last.then_inc(st_bc, 1)

        pe.wait_ge(in_small, 64)
        pe.wait_ge(silu_done, 1)
        for m in range(N_PE_MOD):
            pe.wait_ge(in_ada[m % 8], 16 * (m // 8 + 1))
            for k in range(KD):
                last = nc.tensor.matmul(ps[:, 5, 2 * m:2 * m + 2], ada_ring[:, m % 8, k * P:(k + 1) * P],
                                        silu_cc[:, k, :], start=k == 0, stop=k == KD - 1)
            last.then_inc(ada_mm, 1)
            if m in NORM_AT:
                job_sum(NORM_AT[m])
            elif m - 1 in NORM_AT:
                job_bcast(NORM_AT[m - 1])

        def project(bank, tile, hb, cols, first):
            pe.wait_ge(t_lo, tile + 1)
            for k in range(KD):
                pe.wait_ge(n_lo, first + k + 1)
                last = mm3(ps[:, bank, 0:cols], pw, (ALL, tile, slice(k * P, (k + 1) * P)),
                           hb, (ALL, k, slice(0, cols)), k == 0, k == KD - 1)
            last.then_inc(pj, 1)

        project(0, 0, hb0, TC, 0)
        project(1, 1, hb0, TC, 0)
        project(2, 0, hb1, HT, KD)
        project(3, 1, hb1, HT, KD)
        job_sum(J_KVC)
        project(4, 2, hb1, HT, KD)
        job_bcast(J_KVC)
        pe.wait_ge(mod_set, 1)
        project(5, 3, hb1, HT, KD)
        job_sum(J_KVA)
        pe.wait_ge(kv_done, 1)
        project(0, 0, hb0, HT, 2 * KD)
        job_bcast(J_KVA)
        pe.wait_ge(kr_in, 1)
        project(1, 1, hb0, HT, 2 * KD)
        job_sum(J_QA)
        pe.wait_ge(kv_done, 2)
        project(2, 2, hb0, HT, 2 * KD)
        job_bcast(J_QA)
        pe.wait_ge(kr_in, 2)
        project(3, 3, hb0, HT, 2 * KD)
        job_sum(J_KVB)
        job_bcast(J_KVB)
        job_sum(J_QB)
        job_bcast(J_QB)
        pe.wait_ge(kv_done, 3)
        pe.wait_ge(q_done, 2)
        for b in range(3):
            if b == 2:
                pe.wait_ge(tok_done, 1)
            for t in range(min(4, KT - 4 * b)):
                last = nc.tensor.transpose(ps[:, 4 + b % 2, t * P:(t + 1) * P],
                                           kvf[:, (4 * b + t) * P:(4 * b + t + 1) * P], ident[:])
            last.then_inc(tok_t, 1)

        kinds = []

        def ring(kind):
            if len(kinds) >= 2:
                if kinds[-2] in SPLIT_KINDS:
                    pe.wait_ge(rd, C.at("rd", int(kinds[-1] in SPLIT_KINDS)))
                else:
                    pe.wait_ge(ra, C.at("ra", 1))
            kinds.append(kind)
            C.add("ra")
            if kind in SPLIT_KINDS:
                C.add("rd")
            return 5 + (len(kinds) - 1) % 2

        def scores_part(gb, j, part):
            par, half = gb // 2, gb % 2
            q = slice(half * HT + j * P, half * HT + (j + 1) * P)
            k0, k1 = (((0, 512), (512, 1024), (1024, 1280)) if j % 2 == 0
                      else ((256, 768), (768, 1280), (0, 256)))[part]
            if part == 0:
                if C.i is not None or C.n["ex"] >= 2:
                    pe.wait_ge(ex, C.at("ex", 1))
                C.add("ex")
                if j == 0 and half == 0:
                    C.add("q_ready")
                    pe.wait_ge(q_ready, C.at("q_ready"))
            if part == 2 and (C.i is not None or C.n["ex"] >= 2):
                pe.wait_ge(ex, C.at("ex", 1))
            dst = flat[:, TK * (j % 2) + k0:TK * (j % 2) + k1]
            nc.tensor.matmul(dst, qa[par][0][:, q], ckv_hi[:, k0:k1], start=True, stop=False)
            nc.tensor.matmul(dst, qa[par][1][:, q], ckv_hi[:, k0:k1], start=False, stop=False)
            nc.tensor.matmul(dst, qa[par][0][:, q], ckv_lo[:, k0:k1], start=False, stop=False)
            nc.tensor.matmul(dst, qr[par][:, q], kr_hi[:, k0:k1], start=False, stop=False)
            return nc.tensor.matmul(dst, qr[par][:, q], kr_lo[:, k0:k1], start=False, stop=True)

        def query_item(kind, k):
            bank = ring(kind)
            if kind == "W":
                C.add("hw_l")
                pe.wait_ge(hw_l, C.at("hw_l"))
                for i2 in range(QK):
                    last = mm3(ps[:, bank, i2 * P:(i2 + 1) * P], (hw_hi, hw_lo), (ALL, slice(i2 * P, (i2 + 1) * P)),
                               (hw_hi, hw_lo), (ALL, slice(2 * P, 3 * P)), True, True)
            elif kind == "R":
                for i2 in range(QK):
                    last = mm3(ps[:, bank, :], (hw_hi, hw_lo), (ALL, slice(3 * P + i2 * P, 4 * P + i2 * P)),
                               (qn_hi, qn_lo), (ALL, i2, HALF[k]), i2 == 0, i2 == QK - 1)
            else:
                pe.wait_ge(rd, C.at("rd", 1 + k))
                for i2 in range(QK):
                    last = mm3(ps[:, bank, :], (wa_hi, wa_lo), (ALL, i2, ALL),
                               (qn_hi, qn_lo), (ALL, i2, HALF[k]), i2 == 0, i2 == QK - 1)
            last.then_inc(rg, 1)

        def value_up(par):
            bank = ring("OH")
            pe.wait_ge(ol_l, C.at("ol_l", -1))
            mm3(ps[:, bank, :], uv[par], (ALL, ALL), (olat_hi, olat_lo), (ALL, ALL), True, True).then_inc(rg, 1)

        def group(gb, last_pass):
            turned = []
            for kind, k, part in script_of(gb, last_pass):
                if kind == "S":
                    last = scores_part((gb + 1) % 4, k, part)
                    if part == 2:
                        last.then_inc(s_mm, 1)
                elif kind == "T":
                    if k == 0:
                        pe.wait_ge(ex, C.at("ex"))
                    bank = ring("T")
                    for j in range(4):
                        last = nc.tensor.transpose(ps[:, bank, j * P:(j + 1) * P],
                                                   pbuf[:, 4 * (gb % 2) + j, k * P:(k + 1) * P], ident[:])
                    last.then_inc(rg, 1)
                    turned.append(C.n["rd"])
                elif kind == "PV":
                    if k == 0:
                        C.add("ol_l")
                        pe.wait_ge(ol_l, C.at("ol_l"))
                    pe.wait_ge(rd, C.at("rd", C.n["rd"] - turned[k]))
                    mm3(ps[:, 7, :], (tok_hi, tok_lo), (ALL, k, ALL), (pt_hi, pt_lo),
                        (ALL, (10 * gb + k) % 4, ALL), k == 0, k == KT - 1).then_inc(pv, 1)
                elif kind in ("M", "X", "V"):
                    continue
                elif kind == "OH":
                    value_up(value_parity(gb))
                elif kind == "B":
                    C.add("ri", 4)
                    pe.wait_ge(ri, C.at("ri"))
                    bank = ring("B")
                    for j in range(4):
                        last = nc.tensor.matmul(ps[:, bank, j * P:(j + 1) * P], ones[:], inv_diag[:, j, :],
                                                start=True, stop=True)
                    last.then_inc(rg, 1)
                else:
                    query_item(kind, k)

        pe.wait_ge(tok_done, 3)
        pe.wait_ge(q_done, 4)
        pe.wait_ge(kr_done, 3)
        for kind, k in QUERY_STAGE:
            query_item(kind, k)
        for n in range(12):
            last = scores_part(0, n // 3, n % 3)
            if n % 3 == 2:
                last.then_inc(s_mm, 1)
            elif n % 3 == 0:
                last.then_inc(pv, 1)
        passes = HEADS // 2 - 1
        with pe.Fori(0, passes) as i:
            C.enter(i, {"ra": RING_PASS, "rd": SPLIT_PASS, "ex": 16, "q_ready": 2, "hw_l": 2, "ri": 16, "ol_l": 4})
            for gb in range(4):
                group(gb, False)
            C.leave(passes)
        for gb in range(4):
            group(gb, True)
        value_up(1)

        C.n["t_lo"] = PRO_TILES

        def down(blk, slot, stats, ready):
            for half in range(2):
                pe.wait_ge(gl, ready[half] + blk * 4)
                for m in range(KD):
                    if not isinstance(blk, int) or blk > 0 or 8 * half + m > 3:
                        pe.wait_ge(xe, blk * 16 + (8 * half + m - 3))
                    for f in range(2):
                        last = mm3(ps[:, 4 + m % 4, :], (w_hi, w_lo), (ALL, slot + f, slice(m * P, (m + 1) * P)),
                                   (g_hi, g_lo), (ALL, f, HALF[half]), f == 0, f == 1)
                    last.then_inc(dn, 1)
                    if stats is not None and half == 1 and m == 2:
                        job_sum(stats)
                    if stats is not None and half == 1 and m == 4:
                        job_bcast(stats)

        def inner(bank, slot, half, h_at):
            for k in range(KD):
                pe.wait_ge(n_lo, h_at + half * KD + k + 1)
                last = mm3(ps[:, bank, :], (w_hi, w_lo), (ALL, slot, slice(k * P, (k + 1) * P)),
                           h, (ALL, k, HALF[half]), k == 0, k == KD - 1)
            last.then_inc(pj, 1)

        def ffn_block(blk, h_at, first, stats_b, stats):
            for f in range(2):
                C.add("t_lo", 2)
                pe.wait_ge(t_lo, C.at("t_lo"))
                for half in range(2):
                    if not (first and f == 0):
                        pe.wait_ge(sil, C.at("sil", 1))
                        pe.wait_ge(gm, C.at("gm", 1))
                    C.add("sil")
                    C.add("gm")
                    inner(2 * half, 2 * f, half, h_at)
                    if first and f == 0 and half == 0:
                        job_sum(stats_b)
                    inner(2 * half + 1, 2 * f + 1, half, h_at)
                    if first and f == 0 and half == 0:
                        job_bcast(stats_b)
            C.add("t_lo", 2)
            pe.wait_ge(t_lo, C.at("t_lo"))
            down(blk, 4, stats, (3, 4))

        READER = ("cs", "cs", "zm", "zm", "cs", "cs")

        def conv_block(blk, h_at, first, stats_b, stats):
            for e in range(12):
                if e % 6 == 0:
                    C.add("t_lo", 3)
                    pe.wait_ge(t_lo, C.at("t_lo"))
                if not (first and e < 4):
                    before = [READER[k % 6] for k in range(e + 8, e + 12)]
                    name = before[0]
                    pe.wait_ge(cs if name == "cs" else zm, C.at(name, before.count(name) - 1))
                inner(e % 4, 3 * (e // 6) + (e % 6) // 2, e % 2, h_at)
                C.add(READER[e % 6])
                if first and e == 0:
                    job_sum(stats_b)
                    job_bcast(stats_b)
            C.add("t_lo", 2)
            pe.wait_ge(t_lo, C.at("t_lo"))
            down(blk, 6, stats, (3, 4))

        job = J_MIX
        for b in range(OUT_BLOCKS):
            pe.wait_ge(t_lo, PRO_TILES + OUT_NEEDS[b])
            down(b, 4 + 2 * (b % 2), job if b == OUT_BLOCKS - 1 else None, (2, 4))
        C.n["t_lo"] = PRO_TILES + N_OUT_TILES - 6
        h_at = 3 * KD
        for kind, blocks, first_blk, _ in PHASES[1:]:
            body, per = (ffn_block, {"t_lo": 6, "sil": 4, "gm": 4}) if kind == "ffn" \
                else (conv_block, {"t_lo": 8, "cs": 8, "zm": 4})
            body(first_blk, h_at, True, job + 1, None)
            with pe.Fori(0, blocks - 2) as i:
                C.enter(i, per)
                body(i + (first_blk + 1), h_at, False, None, None)
                C.leave(blocks - 2)
            job += 2
            body(first_blk + blocks - 1, h_at, False, None, job)
            h_at += 2 * KD
        job_sum(job + 1)
        job_bcast(job + 1)

    @block.scalar
    def _(act):
        C = Counts()
        copy = nc.scalar.copy

        def squares(j, m, src, cols):
            if m == 0:
                if j >= 2:
                    act.wait_ge(st_sum, j - 1)
                dst = acc[j % 2][:, 0:cols]
            else:
                if C.n["sqa"] >= 2:
                    act.wait_ge(sqa, C.at("sqa", 1))
                C.add("sqa")
                dst = sq[C.n["sqa"] % 2][:, 0:cols]
            nc.scalar.activation(dst, src, ACT.Square).then_inc(sqd, 1)

        def job_sqrt(j):
            n = job_cols(j) // P
            act.wait_ge(st_sum, j + 1)
            if j >= 1:
                act.wait_ge(st_dg, j)
            nc.scalar.activation(sd[:, 0:n], ps[:, job_banks(j)[0], 0:n], ACT.Sqrt, bias=eps_c[:, 0:1],
                                 scale=1.0 / job_n(j)).then_inc(st_sd, 1)

        def job_out(j):
            act.wait_ge(st_bc, j + 1)
            copy(rstd[j % 2][:, 0:job_cols(j)], ps[:, job_banks(j)[1], 0:job_cols(j)]).then_inc(st_rs, 1)

        def affine(cols, scale, shift):
            C.add("n_mul")
            act.wait_ge(n_mul, C.at("n_mul"))
            t = tmp[(C.n["n_mul"] - 1) % 2][:, 0:cols]
            nc.scalar.activation(t, t, ACT.Identity, bias=shift, scale=scale).then_inc(n_aff, 1)

        def tile_hi(dst, k, *free):
            C.add(f"in_raw{k}", 16)
            act.wait_ge(in_raw[k], C.at(f"in_raw{k}"))
            for sem_value in free:
                act.wait_ge(*sem_value)
            copy(dst, raw[k][:]).then_inc(t_hi, 1)

        act.wait_ge(in_small, 64)
        act.wait_ge(const_set, 1)
        nc.scalar.activation(silu_cc[:], cc_sb[:], ACT.Silu).then_inc(silu_done, 1)
        act.wait_ge(in_ctx, 16)
        for m in range(KD):
            squares(J_CTX, m, ctx_sb[:, m, :], TC)
        for j in (J_XA, J_XB):
            job_sqrt(j - 1)
            job_out(j - 1)
            act.wait_ge(in_xh[j - 1], 16)
            for m in range(KD):
                squares(j, m, x[:, m, HALF[j - 1]], HT)
        job_sqrt(J_XB)
        for k in range(2):
            tile_hi(pw[0][:, k, :], k)
        act.wait_ge(mod_set, 1)
        for k in range(KD):
            affine(TC, svec[:, 0, k:k + 1], ctx_mod[:, k:k + 1])
        job_out(J_XB)
        for k in range(2):
            tile_hi(pw[0][:, 2 + k, :], k)

        def kv_squares(j, bank, n_pj):
            act.wait_ge(pj, n_pj)
            act.wait_ge(st_sum, j - 1)
            nc.scalar.activation(acc[j % 2][:, 0:job_cols(j)], ps[:, bank, 0:job_cols(j)], ACT.Square)\
                .then_inc(kv_sq, 1)

        def q_squares(j, bank, n_pj):
            act.wait_ge(pj, n_pj)
            act.wait_ge(st_sum, j - 1)
            act.wait_ge(sqa, 3 * (KD - 1))
            if j == J_QB:
                act.wait_ge(q_acc, 1)
            nc.scalar.activation(acc[j % 2][:], ps[:, bank, :], ACT.Square).then_inc(q_sq, 1)
            nc.scalar.activation(sq[0][:], ps[:, bank + 1, :], ACT.Square).then_inc(q_sq, 1)

        def keys_in(n, bank, cols, n_pj):
            act.wait_ge(pj, n_pj)
            if n == 2:
                act.wait_ge(kr_done, 1)
            copy(rsb[n % 2][:, 0:cols], ps[:, bank, 0:cols]).then_inc(kr_in, 1)

        for k in range(KD):
            affine(HT, svec[:, 1, k:k + 1], mods[:, k:k + 1])
        kv_squares(J_KVC, 0, 1)
        keys_in(0, 1, TC, 2)
        job_sqrt(J_KVC)
        job_out(J_KVC)
        for k in range(KD):
            affine(HT, svec[:, 1, k:k + 1], mods[:, k:k + 1])
        kv_squares(J_KVA, 2, 3)
        keys_in(1, 3, HT, 4)
        job_sqrt(J_KVA)
        job_out(J_KVA)
        q_squares(J_QA, 4, 6)
        job_sqrt(J_QA)
        act.wait_ge(kv_done, 1)
        job_out(J_QA)
        kv_squares(J_KVB, 0, 7)
        keys_in(2, 1, HT, 8)
        job_sqrt(J_KVB)
        act.wait_ge(kv_done, 2)
        job_out(J_KVB)
        q_squares(J_QB, 2, 10)
        job_sqrt(J_QB)
        act.wait_ge(q_done, 2)
        job_out(J_QB)
        for b in range(3):
            n = min(4, KT - 4 * b)
            act.wait_ge(tok_t, b + 1)
            copy(tok_hi[:, 4 * b:4 * b + n, :].rearrange("p k n -> p (k n)"), ps[:, 4 + b % 2, 0:n * P])\
                .then_inc(tok_h, 1)

        act.wait_ge(in_row, 16)
        nc.scalar.activation(row_a[:], row_a[:], ACT.Silu).then_inc(silu_done, 1)
        entries = [0]

        def ring_out(kind, k, gb, par, group_n):
            bank = 5 + entries[0] % 2
            entries[0] += 1
            C.add("rg")
            act.wait_ge(rg, C.at("rg"))
            if kind == "W":
                copy(wa_hi[:].rearrange("p k n -> p (k n)"), ps[:, bank, 0:QK * P]).then_inc(ra, 1)
            elif kind == "Q":
                copy(qa[par][0][:, HALF[k]], ps[:, bank, :]).then_inc(ra, 1)
            elif kind == "R":
                if C.i is not None or C.n["q_rd"] >= 2:
                    act.wait_ge(q_ready, C.at("q_ready"))
                C.add("q_rd")
                copy(qsb[k][:], ps[:, bank, :]).then_inc(ra, 1)
            elif kind == "T":
                C.add("pv")
                act.wait_ge(pv, C.at("pv"))
                copy(pt_hi[:, (10 * gb + k) % 4, :], ps[:, bank, :]).then_inc(ra, 1)
            elif kind == "B":
                copy(inv_rows[:], ps[:, bank, :]).then_inc(ra, 1)
            else:
                copy(o[:, group_n, :] if isinstance(group_n, int)
                     else o[:, bass.ds(group_n, 1), :].rearrange("p a n -> p (a n)"), ps[:, bank, :]).then_inc(ra, 1)

        def head_hi(par):
            C.add("in_head", 16)
            act.wait_ge(in_head, C.at("in_head"))
            copy(hw_hi[:], hraw[:, 0:HW]).then_inc(hw_h, 1)
            copy(uv[par][0][:], hraw[:, HW:HW + P]).then_inc(hw_h, 1)

        def exp_tile(gb, j):
            C.add("mx")
            act.wait_ge(mx, C.at("mx"))
            buf = 4 * (gb % 2) + j
            nc.scalar.activation(pbuf[:, buf, :], flat[:, TK * (j % 2):TK * (j % 2 + 1)], ACT.Exp,
                                 bias=nmax[:, j % 2:j % 2 + 1], scale=SCALE, accum_out=rsum[:, buf:buf + 1])\
                .then_inc(ex, 1)

        def group(gb, last_pass, group_n):
            for kind, k, part in script_of(gb, last_pass):
                if kind == "X":
                    exp_tile((gb + 1) % 4, k)
                elif kind == "PV":
                    if k in MOD_AT:
                        n = 2 * gb + MOD_AT[k]
                        C.add("mod_p")
                        act.wait_ge(mod_p, C.at("mod_p"))
                        nc.scalar.activation(mod_prod[:], mod_prod[:], ACT.Copy, accum_out=mod_new[:, n:n + 1])\
                            .then_inc(mod_c, 1)
                        C.add("mod_c")
                elif kind in RING_KINDS:
                    ring_out(kind, k, gb, (gb // 2 + 1) % 2, group_n)
                    if kind == "OH" and has_query(gb, last_pass):
                        head_hi((gb // 2 + 1) % 2)
                    if kind == "R" and k == 1:
                        C.add("q_ready")

        def mods_to_place(i):
            act.wait_ge(mod_c, C.at("mod_c"))
            copy(cols_of(mods, i * 8 + N_PE_MOD, 8), mod_new[:]).then_inc(mod_out, 1)
            C.add("mod_out")

        head_hi(0)
        for kind, k in QUERY_STAGE:
            ring_out(kind, k, 0, 0, 0)
        C.n["q_ready"] = 1
        for j in range(4):
            exp_tile(0, j)
        passes = HEADS // 2 - 1
        with act.Fori(0, passes) as i:
            C.enter(i, {"rg": RING_PASS, "mx": 16, "in_head": 32, "q_rd": 4, "q_ready": 2, "pv": 40,
                        "mod_p": 8, "mod_c": 8, "mod_out": 1})
            for gb in range(4):
                group(gb, False, i * 4 + gb)
            mods_to_place(i)
            C.leave(passes)
        for gb in range(4):
            group(gb, True, 4 * passes + gb)
        mods_to_place(passes)
        ring_out("OH", 0, 0, 0, 2 * HEADS)

        C.n["sqa"] = 3 * (KD - 1)

        def turn(blk, j, after, tail):
            shift, row = after
            for m in range(KD):
                act.wait_ge(xe, 16 * blk + m + 1)
                squares(j, m, x[:, m, HALF[0]], HT)
            job_sqrt(j)

            def squares_b(m):
                act.wait_ge(xe, 16 * blk + KD + m + 1)
                squares(j + 1, m, x[:, m, HALF[1]], HT)

            for m in range(2):
                squares_b(m)
            job_out(j)
            act.wait_ge(sv_set, row // 2)
            for k in range(KD):
                affine(HT, svec[:, row, k:k + 1], mods[:, shift + k:shift + k + 1])
                if k + 2 < KD:
                    squares_b(k + 2)
            tail()
            job_sqrt(j + 1)
            job_out(j + 1)
            for k in range(KD):
                affine(HT, svec[:, row, k:k + 1], mods[:, shift + k:shift + k + 1])

        def split_head(b, f, half):
            if b >= 1:
                act.wait_ge(dn, 16 * (b - 1) + 8 * half + 8)
            elif f == 0 and half == 0:
                act.wait_ge(ra, RING_ALL)
            copy(g_hi[:, f, HALF[half]], o[:, 1 + 4 * b + 2 * f + half, :]).then_inc(o_h, 1)

        def out_tiles(step):
            for k, (slot, over) in enumerate(OUT_TILES[step]):
                tile_hi(w_hi[:, slot, :], k, *([(dn, 16 * over)] if over else []))

        out_tiles(0)
        for b in range(OUT_BLOCKS):
            for half in range(2):
                for f in range(2):
                    split_head(b, f, half)
                if b >= 1:
                    out_tiles(2 * b - 1 + half)
            if b == 1:
                act.wait_ge(in_row, 32)
                nc.scalar.activation(row_f[:], row_f[:], ACT.Silu).then_inc(silu_done, 1)
        turn(OUT_BLOCKS - 1, J_MIX, AFTER[0], lambda: None)
        C.n["pj"], C.n["gl"] = 10, 4 * OUT_BLOCKS

        def ffn_block(blk, prefetch, prefetch_down):
            for f in range(2):
                for half in range(2):
                    C.add("pj", 2)
                    act.wait_ge(pj, C.at("pj", 1))
                    act.wait_ge(gl, C.at("gl", 1))
                    C.add("gl")
                    nc.scalar.activation(ab[half][:], ps[:, 2 * half, :], ACT.Silu).then_inc(sil, 1)
                if prefetch:
                    for k in range(2):
                        tile_hi(w_hi[:, 2 * f + k, :], k, (pj, C.at("pj")))
            if prefetch_down:
                down_tiles(blk)

        def down_tiles(blk):
            for k in range(2):
                tile_hi(w_hi[:, 4 + k, :], k, (dn, blk * 16 + 16))

        def conv_block(blk):
            for k in range(2):
                tile_hi(w_hi[:, 6 + k, :], k, (dn, blk * 16))
            for f in range(2):
                for e in range(6):
                    C.add("pj")
                    half, bank = e % 2, (6 * f + e) % 4
                    if e // 2 == 1:
                        continue
                    act.wait_ge(pj, C.at("pj"))
                    if e == 0:
                        act.wait_ge(gl, C.at("gl"))
                    copy(ab[half][:] if e < 2 else bsb[:, HALF[half]], ps[:, bank, :]).then_inc(cs, 1)
                C.add("gl", 2)
                for k in range(3):
                    tile_hi(w_hi[:, 3 * f + k, :], (3 * f + k) % 2, (pj, C.at("pj")))

        job = J_MIX + 2
        for p, (kind, blocks, first_blk, _) in enumerate(PHASES[1:], 1):
            last = first_blk + blocks - 1
            if kind == "ffn":
                with act.Fori(0, blocks - 1) as i:
                    C.enter(i, {"pj": 8, "gl": 4, "in_raw0": 48, "in_raw1": 48})
                    ffn_block(i + first_blk, True, True)
                    C.leave(blocks - 1)
                ffn_block(last, p < 3, False)
            else:
                with act.Fori(0, blocks) as i:
                    C.enter(i, {"pj": 12, "gl": 4, "in_raw0": 64, "in_raw1": 64})
                    conv_block(i + first_blk)
                    C.leave(blocks)
            if p < 3:
                turn(last, job, AFTER[p], (lambda last=last: down_tiles(last)) if kind == "ffn" else (lambda: None))
            else:
                for half in range(2):
                    for m in range(KD):
                        act.wait_ge(xe, 16 * last + 8 * half + m + 1)
                        squares(job + half, m, x[:, m, HALF[half]], HT)
                    job_sqrt(job + half)
                    job_out(job + half)
            job += 2

    @block.vector
    def _(dve):
        C = Counts()

        def own(ins):
            ins.then_inc(v, 1)
            C.add("v")
            dve.wait_ge(v, C.at("v"))

        def lo_part(dst, full, hi):
            return nc.vector.tensor_tensor(dst, full, hi.bitcast(F32), ALU.subtract)

        def job_diag(j):
            n = job_cols(j) // P
            dve.wait_ge(st_sd, j + 1)
            own(nc.vector.reciprocal(rr[:, 0:n], sd[:, 0:n]))
            if j >= 1:
                dve.wait_ge(st_bc, j)
            for t in range(n):
                last = nc.vector.tensor_scalar(diag[:, t, :], ident[:], rr[:, t:t + 1], None, ALU.mult)
            last.then_inc(st_dg, 1)

        def apply(dst, k, cols):
            C.add("n_aff")
            dve.wait_ge(n_aff, C.at("n_aff"))
            t = tmp[(C.n["n_aff"] - 1) % 2][:, 0:cols.stop - cols.start]
            own(nc.vector.tensor_copy(dst[0][:, k, cols], t))
            lo_part(dst[1][:, k, cols], t, dst[0][:, k, cols]).then_inc(n_lo, 1)

        def tile_lo(dst, hi, k):
            C.add("t_hi")
            dve.wait_ge(t_hi, C.at("t_hi"))
            lo_part(dst, raw[k][:], hi).then_inc(t_lo, 1)

        nc.vector.memset(eps_c[:], EPS).then_inc(const_set, 1)
        for j in (J_CTX, J_XA, J_XB):
            job_diag(j)
        for k in range(2):
            tile_lo(pw[1][:, k, :], pw[0][:, k, :], k)
        dve.wait_ge(ada_mm, N_PE_MOD)
        both = ps[:, 5, 0:2 * N_PE_MOD].rearrange("p (m j) -> p j m", j=2)
        own(nc.vector.tensor_tensor(mods[:, 0:N_PE_MOD], both[:, 0, :], adab[:, 0:N_PE_MOD], ALU.add))
        own(nc.vector.tensor_tensor(ctx_mod[:], both[:, 1, :], adab[:, 0:N_PE_MOD], ALU.add))

        def scale_vec(row, mod_scale, w):
            return nc.vector.scalar_tensor_tensor(out=svec[:, row, :], in0=mod_scale, scalar=1.0,
                                                  in1=norm_w[:, w * KD:(w + 1) * KD], op0=ALU.add, op1=ALU.mult)
        own(scale_vec(0, ctx_mod[:, KD:2 * KD], 0))
        scale_vec(1, mods[:, KD:2 * KD], 0).then_inc(mod_set, 1)
        dve.wait_ge(mod_set, 1)
        for k in range(KD):
            apply(hb0, k, slice(0, TC))
        for k in range(2):
            tile_lo(pw[1][:, 2 + k, :], pw[0][:, 2 + k, :], k)
        for k in range(KD):
            apply(hb1, k, slice(0, HT))

        def latents(j, bank, at):
            n = job_cols(j)
            dve.wait_ge(st_rs, j + 1)
            own(nc.vector.scalar_tensor_tensor(out=kvf[:, at:at + n], in0=ps[:, bank, 0:n], scalar=kvn_w,
                                               in1=rstd[j % 2][:, 0:n], op0=ALU.mult, op1=ALU.mult))
            own(nc.vector.tensor_copy(ckv_hi[:, at:at + n], kvf[:, at:at + n]))
            own(lo_part(ckv_lo[:, at:at + n], kvf[:, at:at + n], ckv_hi[:, at:at + n]))
            nc.vector.memset(mx_raw[:], 0.0).then_inc(kv_done, 1)

        def keys(n, at, cols, rotate):
            dve.wait_ge(kr_in, n + 1)
            if rotate:
                nc.vector.stream_shuffle(rsh[n % 2][:], rsb[n % 2][:], MASK16).then_inc(kr_sh, 1)
                dve.wait_ge(kr_rot, n)
            own(nc.vector.tensor_copy(kr_hi[:, at:at + cols], rsb[n % 2][:, 0:cols]))
            lo_part(kr_lo[:, at:at + cols], rsb[n % 2][:, 0:cols], kr_hi[:, at:at + cols]).then_inc(kr_done, 1)

        def queries(j, bank, half):
            dve.wait_ge(st_rs, j + 1)
            for k in range(QK):
                own(nc.vector.scalar_tensor_tensor(out=tmp[k][:], in0=ps[:, bank + k, :], scalar=qn_w[:, k:k + 1],
                                                   in1=rstd[j % 2][:], op0=ALU.mult, op1=ALU.mult))
                own(nc.vector.tensor_copy(qn_hi[:, k, HALF[half]], tmp[k][:]))
                lo_part(qn_lo[:, k, HALF[half]], tmp[k][:], qn_hi[:, k, HALF[half]]).then_inc(q_done, 1)

        job_diag(J_KVC)
        latents(J_KVC, 0, T)
        keys(0, T, TC, False)
        dve.wait_ge(pj, 2)
        for k in range(KD):
            apply(hb0, k, slice(0, HT))
        job_diag(J_KVA)
        latents(J_KVA, 2, 0)
        keys(1, 0, HT, True)
        job_diag(J_QA)
        queries(J_QA, 4, 0)
        job_diag(J_KVB)
        latents(J_KVB, 0, HT)
        keys(2, HT, HT, True)
        job_diag(J_QB)
        queries(J_QB, 2, 1)
        for b in range(3):
            n = min(4, KT - 4 * b)
            dve.wait_ge(tok_h, b + 1)
            lo_part(tok_lo[:, 4 * b:4 * b + n, :].rearrange("p k n -> p (k n)"), ps[:, 4 + b % 2, 0:n * P],
                    tok_hi[:, 4 * b:4 * b + n, :].rearrange("p k n -> p (k n)")).then_inc(tok_done, 1)

        own(nc.vector.memset(olat_hi[:].bitcast(F32), 0.0))
        for t in uv[1]:
            own(nc.vector.memset(t[:].bitcast(F32), 0.0))
        nc.vector.memset(olat_lo[:].bitcast(F32), 0.0).then_inc(ol_l, 1)
        C.n["pv"] = 4
        entries = [0]

        def ring_lo(kind, k, gb, par):
            bank = 5 + entries[0] % 2
            entries[0] += 1
            C.add("ra")
            if kind in ("OH", "B"):
                return
            dve.wait_ge(ra, C.at("ra"))
            if kind == "R":
                dve.sem_inc(wait_end, 1)
            if kind == "W":
                lo_part(wa_lo[:].rearrange("p k n -> p (k n)"), ps[:, bank, 0:QK * P],
                        wa_hi[:].rearrange("p k n -> p (k n)")).then_inc(rd, 1)
            elif kind == "R":
                nc.vector.stream_shuffle(qsh[k][:], qsb[k][:], MASK16).then_inc(q_sh, 1)
            elif kind == "T":
                slot = (10 * gb + k) % 4
                lo_part(pt_lo[:, slot, :], ps[:, bank, :], pt_hi[:, slot, :]).then_inc(rd, 1)
            else:
                lo_part(qa[par][1][:, HALF[k]], ps[:, bank, :], qa[par][0][:, HALF[k]]).then_inc(rd, 1)
                C.add("q_rot")
                dve.wait_ge(q_rot, C.at("q_rot"))
                q = qr[par]
                own(nc.vector.tensor_copy(q[:, HALF[k]], qsb[k][:]))
                low = q[64:128, HALF[k]]
                last = lo_part(low, qsb[k][64:128, :], low)
                if k == 0:
                    own(last)
                else:
                    last.then_inc(q_ready, 1)

        def head_lo(par):
            C.add("hw_h", 2)
            dve.wait_ge(hw_h, C.at("hw_h"))
            own(lo_part(hw_lo[:], hraw[:, 0:HW], hw_hi[:]))
            lo_part(uv[par][1][:], hraw[:, HW:HW + P], uv[par][0][:]).then_inc(hw_l, 1)

        def row_max(j):
            C.add("s_mm")
            dve.wait_ge(s_mm, C.at("s_mm"))
            own(nc.vector.tensor_reduce(mx_raw[:, j % 2:j % 2 + 1], flat[:, TK * (j % 2):TK * (j % 2 + 1)], AX_X,
                                        ALU.max))
            nc.vector.tensor_scalar(nmax[:, j % 2:j % 2 + 1], mx_raw[:, j % 2:j % 2 + 1], -SCALE, None, ALU.mult)\
                .then_inc(mx, 1)

        def row_inverse(gb, j):
            C.add("ex")
            dve.wait_ge(ex, C.at("ex"))
            buf = 4 * (gb % 2) + j
            own(nc.vector.reciprocal(rinv[:, buf:buf + 1], rsum[:, buf:buf + 1]))
            nc.vector.tensor_scalar(inv_diag[:, j, :], ident[:], rinv[:, buf:buf + 1], None, ALU.mult)\
                .then_inc(ri, 1)

        def group(gb, last_pass):
            for kind, k, _ in script_of(gb, last_pass):
                if kind == "M":
                    row_max(k)
                elif kind == "V":
                    row_inverse((gb + 1) % 4, k)
                elif kind == "PV":
                    if k == KT - 1:
                        C.add("pv", KT)
                        dve.wait_ge(pv, C.at("pv"))
                        dve.wait_ge(ra, C.at("ra"))
                        own(nc.vector.tensor_tensor(olat[:], ps[:, 7, :], inv_rows[:], ALU.mult))
                        own(nc.vector.tensor_copy(olat_hi[:], olat[:]))
                        lo_part(olat_lo[:], olat[:], olat_hi[:]).then_inc(ol_l, 1)
                elif kind in RING_KINDS:
                    ring_lo(kind, k, gb, (gb // 2 + 1) % 2)
                    if kind == "OH" and has_query(gb, last_pass):
                        head_lo((gb // 2 + 1) % 2)

        head_lo(0)
        for kind, k in QUERY_STAGE:
            ring_lo(kind, k, 0, 0)
        for j in range(4):
            row_max(j)
            row_inverse(0, j)
        passes = HEADS // 2 - 1
        with dve.Fori(0, passes) as i:
            C.enter(i, {"ra": RING_PASS, "s_mm": 16, "ex": 16, "hw_h": 4, "q_rot": 4, "pv": 40,
                        "v": 16 + 2 * 4 + 16 + 2 * 4})
            for gb in range(4):
                group(gb, False)
            C.leave(passes)
        for gb in range(4):
            group(gb, True)

        def to_x(blk, half, m, gate):
            dve.wait_ge(dn, blk * 16 + (8 * half + m + 1))
            nc.vector.scalar_tensor_tensor(out=x[:, m, HALF[half]], in0=ps[:, 4 + m % 4, :],
                                           scalar=mods[:, gate + m:gate + m + 1], in1=x[:, m, HALF[half]],
                                           op0=ALU.mult, op1=ALU.add).then_inc(xe, 1)

        def turn(blk, j, gate, tail):
            for m in range(KD):
                to_x(blk, 0, m, gate)
            for m in range(4):
                to_x(blk, 1, m, gate)
            job_diag(j)
            for k in range(KD):
                if k + 4 < KD:
                    to_x(blk, 1, k + 4, gate)
                apply(h, k, HALF[0])
            tail()
            job_diag(j + 1)
            for k in range(KD):
                apply(h, k, HALF[1])

        def split_head(b, f, half):
            C.add("o_h")
            dve.wait_ge(o_h, C.at("o_h"))
            lo_part(g_lo[:, f, HALF[half]], o[:, 1 + 4 * b + 2 * f + half, :], g_hi[:, f, HALF[half]]).then_inc(gl, 1)

        gate = PHASES[0][3]
        dve.wait_ge(mod_out, passes + 1)
        own(nc.vector.tensor_tensor(mods[:, N_PE_MOD:N_PE_MOD + N_ATT_MOD], mods[:, N_PE_MOD:N_PE_MOD + N_ATT_MOD],
                                    adab[:, N_PE_MOD:N_PE_MOD + N_ATT_MOD], ALU.add))
        scale_vec(2, mods[:, mod_col(0, SCALE2):mod_col(0, SCALE2) + KD], 1).then_inc(sv_set, 1)
        def out_tiles(step):
            for k, (slot, _) in enumerate(OUT_TILES[step]):
                tile_lo(w_lo[:, slot, :], w_hi[:, slot, :], k)

        out_tiles(0)
        for half in range(2):
            for f in range(2):
                split_head(0, f, half)
        for b in range(OUT_BLOCKS - 1):
            for half in range(2):
                for m in range(KD):
                    if b == half == 0:
                        dve.wait_ge(in_x[m], 16)
                    to_x(b, half, m, gate)
                for f in range(2):
                    split_head(b + 1, f, half)
                out_tiles(1 + 2 * b + half)
        turn(OUT_BLOCKS - 1, J_MIX, gate, lambda: None)
        C.n["pj"], C.n["sil"] = 10, 0

        def ffn_inner(blk, f, half):
            C.add("sil")
            C.add("pj", 2)
            dve.wait_ge(sil, C.at("sil"))
            dve.wait_ge(pj, C.at("pj"))
            C.add("gm")
            nc.vector.tensor_tensor(ab[half][:], ab[half][:], ps[:, 2 * half + 1, :], ALU.mult).then_inc(gm, 1)
            dve.wait_ge(gm, C.at("gm"))
            if f == 0 and half == 0:
                dve.wait_ge(dn, blk * 16)
            own(nc.vector.tensor_copy(g_hi[:, f, HALF[half]], ab[half][:]))
            lo_part(g_lo[:, f, HALF[half]], ab[half][:], g_hi[:, f, HALF[half]]).then_inc(gl, 1)

        def mod_rows(first, end):
            for k in range(first, end):
                C.add("in_modf", 16)
                dve.wait_ge(in_modf, C.at("in_modf"))
                nc.vector.tensor_tensor_reduce(mod_raw_f[:], mod_raw_f[:], row_f[:], 1.0, 0.0, ALU.mult, ALU.add,
                                               mod_new[:, k:k + 1]).then_inc(mod_used, 1)
                C.add("mod_used")

        def down_tiles():
            for k in range(2):
                tile_lo(w_lo[:, 4 + k, :], w_hi[:, 4 + k, :], k)

        def ffn_block(blk, prefetch, mod_count, out_at, gate):
            for f in range(2):
                for half in range(2):
                    ffn_inner(blk, f, half)
                    share = mod_count // 4
                    mod_rows((2 * f + half) * share, (2 * f + half + 1) * share)
                if prefetch:
                    for k in range(2):
                        tile_lo(w_lo[:, 2 * f + k, :], w_hi[:, 2 * f + k, :], k)
            if mod_count:
                dve.wait_ge(mod_used, C.at("mod_used"))
                own(nc.vector.tensor_copy(cols_of(mods, out_at, mod_count), mod_new[:, 0:mod_count]))
            if gate is not None:
                for half in range(2):
                    for m in range(KD):
                        to_x(blk, half, m, gate)
                if prefetch:
                    down_tiles()

        def conv_inner(blk, f, feature):
            for half in range(2):
                C.add("cs")
                dve.wait_ge(cs, C.at("cs", half - 1))
                dve.wait_ge(pj, C.at("pj", -(3 + half)))
                nc.vector.tensor_tensor(zb[:, 1 + half * HT:1 + (half + 1) * HT], ab[half][:],
                                        ps[:, (6 * f + 2 + half) % 4, :], ALU.mult).then_inc(zm, 1)
                C.add("zm")
            dve.wait_ge(zm, C.at("zm"))
            own(nc.vector.tensor_scalar(ub[:], zb[:, 1:T + 1], feature(1), None, ALU.mult))
            for shift in (0, 2):
                own(nc.vector.scalar_tensor_tensor(out=ub[:], in0=zb[:, shift:shift + T], scalar=feature(shift),
                                                   in1=ub[:], op0=ALU.mult, op1=ALU.add))
            for half in range(2):
                C.add("cs")
                dve.wait_ge(cs, C.at("cs"))
                own(nc.vector.tensor_tensor(ub[:, HALF[half]], ub[:, HALF[half]], bsb[:, HALF[half]], ALU.mult))
                if f == 0 and half == 0:
                    dve.wait_ge(dn, blk * 16)
                own(nc.vector.tensor_copy(g_hi[:, f, HALF[half]], ub[:, HALF[half]]))
                lo_part(g_lo[:, f, HALF[half]], ub[:, HALF[half]], g_hi[:, f, HALF[half]]).then_inc(gl, 1)
            C.add("pj", 6)

        def conv_block(blk, col, gate):
            for k in range(2):
                tile_lo(w_lo[:, 6 + k, :], w_hi[:, 6 + k, :], k)
            for f in range(2):
                own(nc.vector.tensor_copy(taps[:], cols_of(conv_w, col + 3 * f, 3)))
                conv_inner(blk, f, lambda tap: taps[:, tap:tap + 1])
                for k in range(3):
                    tile_lo(w_lo[:, 3 * f + k, :], w_hi[:, 3 * f + k, :], (3 * f + k) % 2)
            if gate is not None:
                for half in range(2):
                    for m in range(KD):
                        to_x(blk, half, m, gate)

        job = J_MIX + 2
        for p, (kind, blocks, first_blk, gate) in enumerate(PHASES[1:], 1):
            last = first_blk + blocks - 1
            n_mod = 4 if p == 1 else 0
            if kind == "ffn":
                per = {"sil": 4, "pj": 8, "gm": 4, "t_hi": 6, "v": 4}
                if n_mod:
                    per |= {"in_modf": 64, "mod_used": 4, "v": 5}
                with dve.Fori(0, blocks - 1) as i:
                    C.enter(i, per)
                    ffn_block(i + first_blk, True, n_mod, i * 4 + (N_PE_MOD + N_ATT_MOD), gate)
                    C.leave(blocks - 1)
                ffn_block(last, p < 3, 2 * n_mod, N_PE_MOD + N_ATT_MOD + n_mod * (blocks - 1), None)
            else:
                own(nc.vector.memset(zb[:], 0.0))
                with dve.Fori(0, blocks - 1) as i:
                    C.enter(i, {"t_hi": 8, "cs": 8, "zm": 4, "pj": 12, "v": 16})
                    conv_block(i + first_blk, i * 6, gate)
                    C.leave(blocks - 1)
                conv_block(last, 6 * (blocks - 1), None)
            if p == 1:
                own(nc.vector.tensor_tensor(mods[:, 48:96], mods[:, 48:96], adab[:, 48:96], ALU.add))
                scale_vec(3, mods[:, mod_col(1, SCALE1):mod_col(1, SCALE1) + KD], 2).then_inc(sv_set, 1)
                scale_vec(4, mods[:, mod_col(1, SCALE2):mod_col(1, SCALE2) + KD], 3).then_inc(sv_set, 1)
            if p < 3:
                turn(last, job, gate, down_tiles if kind == "ffn" else (lambda: None))
            else:
                def finish(half, m):
                    nc.vector.scalar_tensor_tensor(out=x[:, m, HALF[half]], in0=x[:, m, HALF[half]],
                                                   scalar=norm_w[:, 4 * KD + m:4 * KD + m + 1],
                                                   in1=rstd[(job + half) % 2][:], op0=ALU.mult, op1=ALU.mult)\
                        .then_inc(fin, 1)
                for m in range(KD):
                    to_x(last, 0, m, gate)
                for m in range(4):
                    to_x(last, 1, m, gate)
                job_diag(job)
                for m in range(4, KD):
                    to_x(last, 1, m, gate)
                dve.wait_ge(st_rs, job + 1)
                for m in range(KD):
                    finish(0, m)
                job_diag(job + 1)
                dve.wait_ge(st_rs, job + 2)
                for m in range(KD):
                    finish(1, m)
            job += 2

    @block.gpsimd
    def _(pool):
        C = Counts()

        def add_squares(j, m, cols):
            C.add("sqd", 2 if m == 1 else 1)
            pool.wait_ge(sqd, C.at("sqd"))
            C.add("sqa")
            nc.gpsimd.tensor_tensor(acc[j % 2][:, 0:cols], acc[j % 2][:, 0:cols], sq[C.n["sqa"] % 2][:, 0:cols],
                                    ALU.add).then_inc(sqa, 1)
            pool.wait_ge(sqa, C.at("sqa"))

        def mul_rstd(j, src, cols):
            if C.n["n_lo"] >= 2:
                pool.wait_ge(n_lo, C.at("n_lo", 1))
            C.add("n_lo")
            pool.wait_ge(st_rs, j + 1)
            nc.gpsimd.tensor_tensor(tmp[(C.n["n_lo"] - 1) % 2][:, 0:cols], src, rstd[j % 2][:, 0:cols], ALU.mult)\
                .then_inc(n_mul, 1)

        for j in (J_CTX, J_XA, J_XB):
            for m in range(1, KD):
                add_squares(j, m, job_cols(j))
        for k in range(KD):
            mul_rstd(J_CTX, ctx_sb[:, k, :], TC)
        for k in range(KD):
            mul_rstd(J_XA, x[:, k, HALF[0]], HT)
        for k in range(KD):
            mul_rstd(J_XB, x[:, k, HALF[1]], HT)

        def rotate(a, b, half, done):
            pool.wait_ge(in_tab, 16)
            nc.gpsimd.tensor_tensor(a, a, tab[:, 0, HALF[half]], ALU.mult).then_inc(gp, 1)
            nc.gpsimd.tensor_tensor(b, b, tab[:, 1, HALF[half]], ALU.mult).then_inc(gp, 1)
            C.add("gp", 2)
            pool.wait_ge(gp, C.at("gp"))
            nc.gpsimd.tensor_tensor(a, a, b, ALU.add).then_inc(done, 1)

        def add_q(n):
            pool.wait_ge(q_sq, 2 * n)
            j = J_QA if n == 1 else J_QB
            nc.gpsimd.tensor_tensor(acc[j % 2][:], acc[j % 2][:], sq[0][:], ALU.add).then_inc(q_acc, 1)

        pool.wait_ge(kr_sh, 1)
        rotate(rsb[1][:], rsh[1][:], 0, kr_rot)
        add_q(1)
        pool.wait_ge(kr_sh, 2)
        rotate(rsb[0][:], rsh[0][:], 1, kr_rot)
        add_q(2)

        def rotate_queries(k):
            C.add("q_sh")
            pool.wait_ge(q_sh, C.at("q_sh"))
            rotate(qsb[k][:], qsh[k][:], k, q_rot)

        def mod_product(k, first):
            C.add(f"in_mod{k}", 16)
            pool.wait_ge(in_mod[k], C.at(f"in_mod{k}"))
            if not first:
                pool.wait_ge(mod_c, C.at("mod_c"))
            C.add("mod_c")
            nc.gpsimd.tensor_tensor(mod_prod[:], mod_raw[:, k, :], row_a[:], ALU.mult).then_inc(mod_p, 1)

        def group(gb, last_pass):
            for kind, k, _ in script_of(gb, last_pass):
                if kind == "R":
                    rotate_queries(k)
                if kind == "PV" and k in MOD_AT:
                    mod_product(MOD_AT[k], False)

        for k in range(2):
            rotate_queries(k)
        pool.wait_ge(silu_done, 2)
        passes = HEADS // 2 - 1
        with pool.Fori(0, passes) as i:
            C.enter(i, {"q_sh": 4, "gp": 8, "in_mod0": 64, "in_mod1": 64, "mod_c": 8})
            for gb in range(4):
                group(gb, False)
            C.leave(passes)
        for gb in range(4):
            group(gb, True)

        for p in range(4):
            j = J_MIX + 2 * p
            for m in range(1, KD):
                add_squares(j, m, HT)
            if p == 3:
                for m in range(1, KD):
                    add_squares(j + 1, m, HT)
                continue
            add_squares(j + 1, 1, HT)
            for k in range(KD):
                mul_rstd(j, x[:, k, HALF[0]], HT)
                if k + 2 < KD:
                    add_squares(j + 1, k + 2, HT)
            for k in range(KD):
                mul_rstd(j + 1, x[:, k, HALF[1]], HT)


def kernel(x, c, ctx, c_ctx, ada_w, ada_b, norm_mix, norm_ffn, mla_w_dq, mla_q_norm, mla_w_uq, mla_w_dkv,
           mla_kv_norm, mla_w_ukv, mla_w_o, conv_w_in, conv_w, conv_w_out, ffn_w_gate, ffn_w_up, ffn_w_down,
           final_norm):
    import concourse.bacc as bacc
    from concourse.bass_utils import run_bass_kernel_spmd

    def cols(w):
        w = np.asarray(w)
        return w.reshape(KD, P, -1, P).transpose(2, 1, 0, 3).reshape(-1, P, D)

    def rows(w):
        return np.asarray(w).reshape(-1, P, D)

    def per_feature(a):
        return np.asarray(a).reshape(-1, P).T

    ada_w = np.asarray(ada_w)
    uq = np.asarray(mla_w_uq)[0].reshape(QL, HEADS, NOPE + ROPE)
    ukv = np.asarray(mla_w_ukv)[0].reshape(KVL, HEADS, NOPE + VH)
    q_rope = uq[:, :, NOPE:].reshape(QK, P, HEADS, ROPE).transpose(2, 1, 0, 3)
    head_w = np.concatenate([
        uq[:, :, :NOPE].transpose(1, 2, 0), ukv[:, :, :NOPE].transpose(1, 2, 0),
        np.concatenate([q_rope, q_rope], axis=3).reshape(HEADS, P, QK * P),
        ukv[:, :, NOPE:].transpose(1, 0, 2)], axis=2)
    dkv = np.asarray(mla_w_dkv)[0]
    k_rope = dkv[:, KVL:]
    dq = cols(np.asarray(mla_w_dq)[0])
    tiles = [cols(dkv[:, :KVL]), cols(np.concatenate([k_rope, k_rope], axis=1)), dq]
    wo = rows(np.asarray(mla_w_o)[0])

    def ffn(layer):
        gate, up, down = cols(ffn_w_gate[layer]), cols(ffn_w_up[layer]), rows(ffn_w_down[layer])
        return [t for i in range(FFN_BLOCKS) for t in (gate[2 * i], up[2 * i], gate[2 * i + 1], up[2 * i + 1],
                                                       down[2 * i], down[2 * i + 1])]
    f0, f1 = ffn(0), ffn(1)
    w_in, w_out = cols(np.asarray(conv_w_in)[0]), rows(np.asarray(conv_w_out)[0])
    conv_in = [w_in[part * KD + t] for t in range(KD) for part in (1, 2, 0)]
    conv = []
    for i in range(CONV_BLOCKS):
        conv += [w_out[2 * i], w_out[2 * i + 1]] + (conv_in[6 * i + 6:6 * i + 12] if i < CONV_BLOCKS - 1 else f1[:6])
    out_tiles = [wo[0], wo[1], wo[2], wo[3], wo[4], wo[5], f0[0], f0[1], wo[6], wo[7], *f0[2:6]]
    stream = np.concatenate(tiles + [np.stack(out_tiles + f0[6:] + conv_in[:6] + conv + f1[6:])])

    taps = np.asarray(conv_w)[0].reshape(3, KD, P).transpose(2, 1, 0).reshape(P, 3 * KD)
    norms = np.stack([np.asarray(norm_mix)[0], np.asarray(norm_ffn)[0], np.asarray(norm_mix)[1],
                      np.asarray(norm_ffn)[1], np.asarray(final_norm)])
    vec = np.concatenate([per_feature(ada_b), per_feature(norms), per_feature(mla_q_norm), per_feature(mla_kv_norm),
                          taps], axis=1)
    both = np.stack([np.asarray(c)[0], np.asarray(c_ctx)], axis=1)
    cc = both.reshape(KD, P, 2).transpose(1, 0, 2).reshape(P, 2 * KD)

    token = np.arange(T)
    place = np.stack([token // 64, token % 64]).astype(np.float32)
    freq = np.float32(10000.0) ** (-np.arange(ROPE // 4, dtype=np.float32) / np.float32(ROPE // 4))
    feature = np.arange(P) % ROPE
    angle = place[feature // 32] * freq[feature % 16][:, None]
    sign = np.where(feature % 32 < 16, -1.0, 1.0).astype(np.float32)[:, None]
    rope = np.concatenate([np.cos(angle), np.sin(angle) * sign], axis=1).astype(np.float32)

    arrays = {
        "x_t": np.asarray(x)[0].T, "ctx_t": np.asarray(ctx)[0].T, "cc": cc, "c_row": np.asarray(c)[0],
        "ada_pe": cols(ada_w[0][:, :2 * D]), "ada_rows": np.concatenate([rows(ada_w[0][:, 2 * D:].T), rows(ada_w[1].T)]),
        "vec": vec, "consts": np.concatenate([np.eye(P, dtype=np.float32), np.ones((P, P), np.float32)], axis=1),
        "rope": rope, "head_w": head_w, "stream": stream}
    nc = bacc.Bacc("TRN2", target_bir_lowering=False, num_devices=1, dynamic_dma_scratch_size=1024)
    arrays = {name: np.ascontiguousarray(a) for name, a in arrays.items()}
    aps = [nc.dram_tensor(name, a.shape, F32, kind="ExternalInput").ap() for name, a in arrays.items()]
    out_t = nc.dram_tensor("out_t", (D, T), F32, kind="ExternalOutput").ap()
    build(nc, *aps, out_t)
    result = run_bass_kernel_spmd(nc, [arrays], core_ids=[0]).results[0]["out_t"]
    return np.ascontiguousarray(result.T)[None]
```
